# Optimizing a Trainium2 kernel written in Bass

```python
import jax, jax.numpy as jnp
from jax import lax
import numpy as np

D_MODEL = 2048
BATCH = 1
SEQ = 256
DEPTH = 1

D_FF = 5632
PLE_DIM = 256
HGRN_WIDTH = D_MODEL // 2
HGRN_HEAD_DIM = 128
HGRN_HEADS = HGRN_WIDTH // HGRN_HEAD_DIM
CHUNK = 64
LRU_WIDTH = D_MODEL - HGRN_WIDTH
LRU_BLOCKS = 8
LRU_BLOCK_DIM = LRU_WIDTH // LRU_BLOCKS
CONV_WIDTH = 4
LRU_C = 8.0
EPS = 1e-6
IN_COLS = 4 * HGRN_WIDTH + 2 * LRU_WIDTH

kernel_name = "hymba_hgrn2_rglru_macaron_block"

def rmsnorm(x, g):
    xf = x.astype(jnp.float32)
    y = xf * lax.rsqrt(jnp.mean(xf * xf, axis=-1, keepdims=True) + EPS)
    return (y * g.astype(jnp.float32)).astype(x.dtype)

def swiglu(h, w_gate, w_up, w_down):
    return (jax.nn.silu(h @ w_gate) * (h @ w_up)) @ w_down

def hgrn2_chunkwise(q, k, v, logf):
    Bn, S, H, dk = q.shape
    dv = v.shape[-1]
    n = S // CHUNK

    def to_chunks(t):
        return t.reshape(Bn, n, CHUNK, H, t.shape[-1]).transpose(1, 0, 3, 2, 4)

    causal = jnp.tril(jnp.ones((CHUNK, CHUNK), dtype=bool))

    def step(state, inp):
        qc, kc, vc, lf = inp
        b = jnp.cumsum(lf, axis=2)
        o_inter = jnp.einsum('bhtk,bhkv->bhtv', qc * jnp.exp(b), state)
        diff = b[:, :, :, None, :] - b[:, :, None, :, :]
        decay = jnp.exp(jnp.where(causal[:, :, None], diff, -jnp.inf))
        scores = jnp.einsum('bhtk,bhtsk,bhsk->bhts', qc, decay, kc)
        o = o_inter + jnp.einsum('bhts,bhsv->bhtv', scores, vc)
        b_last = b[:, :, -1:, :]
        new_state = jnp.exp(b_last[:, :, 0, :])[..., None] * state + jnp.einsum(
            'bhsk,bhsv->bhkv', kc * jnp.exp(b_last - b), vc)
        return new_state, o

    s0 = jnp.zeros((Bn, H, dk, dv), jnp.float32)
    _, o = lax.scan(step, s0, (to_chunks(q), to_chunks(k), to_chunks(v), to_chunks(logf)))
    return o.transpose(1, 0, 3, 2, 4).reshape(Bn, S, H, dv)

def hgrn2_group(q, f_pre, i, g, lb, g_norm):
    Bn, S, _ = q.shape
    shp = (Bn, S, HGRN_HEADS, HGRN_HEAD_DIM)
    f = lb + (1.0 - lb) * jax.nn.sigmoid(f_pre.astype(jnp.float32))
    logf = jnp.log(f)
    k = 1.0 - f
    o = hgrn2_chunkwise(q.astype(jnp.float32).reshape(shp), k.reshape(shp),
                        i.astype(jnp.float32).reshape(shp), logf.reshape(shp))
    o = rmsnorm(o, g_norm) * jax.nn.silu(g.astype(jnp.float32).reshape(shp))
    return o.reshape(Bn, S, HGRN_WIDTH).astype(q.dtype)

def rglru_group(xb, gate, conv_w, conv_b, w_a, b_a, w_x, b_x, lam):
    Bn, S, _ = xb.shape
    xf = xb.astype(jnp.float32)
    xc = lax.conv_general_dilated(
        xf, conv_w.astype(jnp.float32)[:, None, :], window_strides=(1,),
        padding=[(CONV_WIDTH - 1, 0)], dimension_numbers=('NWC', 'WIO', 'NWC'),
        feature_group_count=LRU_WIDTH) + conv_b.astype(jnp.float32)
    xr = xc.reshape(Bn, S, LRU_BLOCKS, LRU_BLOCK_DIM)
    blk = (LRU_BLOCKS, LRU_BLOCK_DIM)
    r = jax.nn.sigmoid(jnp.einsum('bsnc,ncd->bsnd', xr, w_a.astype(jnp.float32))
                       + b_a.astype(jnp.float32).reshape(blk))
    ig = jax.nn.sigmoid(jnp.einsum('bsnc,ncd->bsnd', xr, w_x.astype(jnp.float32))
                        + b_x.astype(jnp.float32).reshape(blk))
    log_a = -LRU_C * r * jax.nn.softplus(-lam.astype(jnp.float32).reshape(blk))
    a = jnp.exp(log_a)
    u = jnp.sqrt(-jnp.expm1(2.0 * log_a)) * (ig * xr)

    def combine(c1, c2):
        a1, b1 = c1
        a2, b2 = c2
        return a1 * a2, a2 * b1 + b2

    _, h = lax.associative_scan(combine, (a, u), axis=1)
    y = h.reshape(Bn, S, LRU_WIDTH) * jax.nn.gelu(gate.astype(jnp.float32))
    return y.astype(xb.dtype)

def setup_inputs(seed: int = 0) -> dict:
    key = jax.random.key(seed)
    ks = jax.random.split(key, 32)
    f32 = jnp.float32

    def nrm(k, shape, fan_in):
        return jax.random.normal(k, shape, f32) * (fan_in ** -0.5)

    def gain(k, shape):
        return 1.0 + 0.05 * jax.random.normal(k, shape, f32)

    def small(k, shape):
        return 0.01 * jax.random.normal(k, shape, f32)

    a8 = jax.random.uniform(ks[20], (DEPTH, LRU_WIDTH), f32, 0.9, 0.999)
    a_base = a8 ** (1.0 / LRU_C)
    lam = jnp.log(a_base) - jnp.log1p(-a_base)

    return {
        "x": jax.random.normal(ks[0], (BATCH, SEQ, D_MODEL), f32),
        "p": jax.random.normal(ks[1], (DEPTH, BATCH, SEQ, PLE_DIM), f32),
        "ffn1_norm": gain(ks[2], (DEPTH, D_MODEL)),
        "ffn1_w_gate": nrm(ks[3], (DEPTH, D_MODEL, D_FF), D_MODEL),
        "ffn1_w_up": nrm(ks[4], (DEPTH, D_MODEL, D_FF), D_MODEL),
        "ffn1_w_down": nrm(ks[5], (DEPTH, D_FF, D_MODEL), D_FF),
        "mix_norm": gain(ks[6], (DEPTH, D_MODEL)),
        "w_in": nrm(ks[7], (DEPTH, D_MODEL, IN_COLS), D_MODEL),
        "hgrn_lower_bounds": 0.5 * jax.random.normal(ks[8], (DEPTH + 1, HGRN_WIDTH), f32),
        "hgrn_g_norm": gain(ks[9], (DEPTH, HGRN_HEAD_DIM)),
        "conv_w": nrm(ks[10], (DEPTH, CONV_WIDTH, LRU_WIDTH), CONV_WIDTH),
        "conv_b": small(ks[11], (DEPTH, LRU_WIDTH)),
        "lru_w_a": nrm(ks[12], (DEPTH, LRU_BLOCKS, LRU_BLOCK_DIM, LRU_BLOCK_DIM), LRU_BLOCK_DIM),
        "lru_b_a": small(ks[13], (DEPTH, LRU_WIDTH)),
        "lru_w_x": nrm(ks[14], (DEPTH, LRU_BLOCKS, LRU_BLOCK_DIM, LRU_BLOCK_DIM), LRU_BLOCK_DIM),
        "lru_b_x": small(ks[15], (DEPTH, LRU_WIDTH)),
        "lru_lambda": lam,
        "w_out": nrm(ks[16], (DEPTH, D_MODEL, D_MODEL), D_MODEL),
        "ffn2_norm": gain(ks[17], (DEPTH, D_MODEL)),
        "ffn2_w_gate": nrm(ks[18], (DEPTH, D_MODEL, D_FF), D_MODEL),
        "ffn2_w_up": nrm(ks[19], (DEPTH, D_MODEL, D_FF), D_MODEL),
        "ffn2_w_down": nrm(ks[21], (DEPTH, D_FF, D_MODEL), D_FF),
        "ple_norm": gain(ks[22], (DEPTH, D_MODEL)),
        "ple_w_gate": nrm(ks[23], (DEPTH, D_MODEL, D_MODEL), D_MODEL),
        "ple_b_gate": small(ks[24], (DEPTH, D_MODEL)),
        "ple_w_proj": nrm(ks[25], (DEPTH, PLE_DIM, D_MODEL), PLE_DIM),
        "final_norm": gain(ks[26], (D_MODEL,)),
    }

def reference(x, p, ffn1_norm, ffn1_w_gate, ffn1_w_up, ffn1_w_down, mix_norm, w_in,
              hgrn_lower_bounds, hgrn_g_norm, conv_w, conv_b, lru_w_a, lru_b_a, lru_w_x,
              lru_b_x, lru_lambda, w_out, ffn2_norm, ffn2_w_gate, ffn2_w_up, ffn2_w_down,
              ple_norm, ple_w_gate, ple_b_gate, ple_w_proj, final_norm):
    lb_all = jnp.cumsum(jax.nn.softmax(hgrn_lower_bounds.astype(jnp.float32), axis=0), axis=0)
    H1, H2, H3, H4 = HGRN_WIDTH, 2 * HGRN_WIDTH, 3 * HGRN_WIDTH, 4 * HGRN_WIDTH
    for l in range(DEPTH):
        h = rmsnorm(x, ffn1_norm[l])
        x = x + 0.5 * swiglu(h, ffn1_w_gate[l], ffn1_w_up[l], ffn1_w_down[l])

        h = rmsnorm(x, mix_norm[l])
        z = h @ w_in[l]
        o_hgrn = hgrn2_group(z[..., :H1], z[..., H1:H2], z[..., H2:H3], z[..., H3:H4],
                             lb_all[l], hgrn_g_norm[l])
        o_lru = rglru_group(z[..., H4:H4 + LRU_WIDTH], z[..., H4 + LRU_WIDTH:],
                            conv_w[l], conv_b[l], lru_w_a[l], lru_b_a[l],
                            lru_w_x[l], lru_b_x[l], lru_lambda[l])
        x = x + jnp.concatenate([o_hgrn, o_lru], axis=-1) @ w_out[l]

        h = rmsnorm(x, ffn2_norm[l])
        x = x + 0.5 * swiglu(h, ffn2_w_gate[l], ffn2_w_up[l], ffn2_w_down[l])

        h = rmsnorm(x, ple_norm[l])
        gate = jax.nn.sigmoid(h @ ple_w_gate[l] + ple_b_gate[l])
        x = x + gate * (p[l] @ ple_w_proj[l])
    return rmsnorm(x, final_norm)


_drawn_inputs = setup_inputs


def setup_inputs(seed=0):
    import zlib

    import numpy as np

    out = dict(_drawn_inputs(seed))
    spreads = {}
    factors = {'hgrn_g_norm': 2.868,
     'conv_b': 3.772,
     'lru_b_a': 64.0,
     'lru_b_x': 64.0,
     'ffn2_norm': 3.384,
     'ple_norm': 160.173,
     'ple_b_gate': 200.0}
    for name, (base, spread) in spreads.items():
        noise = np.random.default_rng([zlib.crc32(name.encode()), seed]).standard_normal(out[name].shape)
        drawn = base * np.exp(spread * noise) if base else spread * noise
        out[name] = __import__('jax').numpy.asarray(drawn.astype(out[name].dtype))
    for name, factor in factors.items():
        out[name] = (out[name] * factor).astype(out[name].dtype)
    return out
```

```python
from contextlib import ExitStack

import concourse.bass as bass
from concourse import mybir

ALU = mybir.AluOpType
ACT = mybir.ActivationFunctionType
AX = mybir.AxisListType
F32 = mybir.dt.float32
F32R = mybir.dt.float32r
BF16 = mybir.dt.bfloat16
I16 = mybir.dt.int16
I32 = mybir.dt.int32

P = 128
TILES = 2
TOK = TILES * P
N = 512
UK = 2
RING = 4
EPS = 1e-6
LEVELS = [1, 2, 4, 8, 16, 32, 64]
SERIES = [15, 13, 11, 9, 7, 5, 3]


class Uses:

    def __init__(self, read):
        self.read, self.readers, self.at = read, [], {}

    def add(self, key, reader):
        self.at[key] = len(self.readers)
        self.readers.append(reader)
        return self.at[key]

    def done(self, index):
        reader = self.readers[index]
        return self.read[reader], self.readers[:index + 1].count(reader)


def block_kernel(nc, A, out):
    D = A["x"].shape[-1]
    FF = A["ffn1_w_gate"].shape[-1]
    PLE = A["p"].shape[-1]
    HW = A["hgrn_lower_bounds"].shape[-1]
    LW = A["conv_w"].shape[-1]
    CONV = A["conv_w"].shape[-2]
    KT = D // P
    XC = D // N
    CT = N // P
    UD = KT // UK
    CH = FF // N
    HALF = [(CH + 1) // 2, CH // 2]
    CHUNK0 = [0, HALF[0]]
    HEADS = HW // P
    NB = LW // P
    assert D == 2048 and FF % N == 0 and HW == LW == D // 2 and A["x"].shape[1] == TOK
    assert HEADS == NB == 8 and PLE == UK * P and CONV == 4 and CT == 4

    x_dram = A["x"].rearrange("b (i p) d -> p (b i) d", p=P)
    p_dram = A["p"].rearrange("l b (i p) d -> p (l b i) d", p=P)
    out_dram = out.rearrange("b (i p) d -> p (b i) d", p=P)
    w_in, w_out = A["w_in"][0], A["w_out"][0]
    w_ple, w_proj = A["ple_w_gate"][0], A["ple_w_proj"][0]
    ffn_w = [[A[f"ffn{f}_w_{n}"][0] for n in ("gate", "up", "down")] for f in (1, 2)]

    DOWN = [HALF[h] * CT // UK for h in range(2)]
    OUT = [6, 2]
    FFN_UNITS = 2 * UD * CH + XC * sum(DOWN)
    U_IN = FFN_UNITS
    U_OUT = [U_IN + UD * 12, U_IN + UD * 12 + XC * OUT[0]]
    U_FFN = [0, U_OUT[1] + XC * OUT[1]]
    U_PROJ = U_FFN[1] + FFN_UNITS
    U_GATE = U_PROJ + XC
    UNITS = U_GATE + XC * UD
    MIX = U_FFN[1] - U_IN

    def ffn_unit(f, half):
        up = U_FFN[f] + half * HALF[0] * 2 * UD + half * XC * DOWN[0]
        return up, up + 2 * UD * HALF[half]

    Z = [("gate", 0, 4 * HW + LW), ("xb", 0, 4 * HW), ("gate", 1, 4 * HW + LW + N), ("xb", 1, 4 * HW + N)]
    for g in range(2):
        Z += [("f", g, HW + g * N), ("q", g, g * N), ("v", g, 2 * HW + g * N), ("g", g, 3 * HW + g * N)]
    TURNED = [ci for ci, z in enumerate(Z) if z[0] in ("gate", "xb", "f", "q")]
    OUT_KT = [list(range(HEADS, KT)) + list(range(4)), list(range(4, HEADS))]
    LRU0 = [16, 32]
    SCORE = {0: 61, 1: 64, 2: 73, 3: 76, 4: 87, 5: 90, 6: 99, 7: 102}
    O_AT = {h: u + 3 for h, u in SCORE.items()}
    Y_AT = {0: 74, 1: 84, 2: 100, 3: 110}
    B_AT, A_AT = {0: 55, 1: 67, 2: 79, 3: 93}, {0: 59, 1: 71, 2: 85, 3: 97}
    GATED_AT = {0: 72, 1: 83, 2: 99, 3: 109}

    with ExitStack() as ctx:
        def sb(name, shape, dt=F32):
            return ctx.enter_context(nc.sbuf_tensor(name, shape, dt))

        def sem(name):
            return ctx.enter_context(nc.semaphore(name))

        x = sb("x_res", [P, TILES, D])
        xt_hi, xt_lo = sb("xt_hi", [P, KT, TOK], F32R), sb("xt_lo", [P, KT, TOK], F32R)
        HT = HALF[0] * CT
        h_hi, h_lo = sb("h_hi", [P, HT, TOK], F32R), sb("h_lo", [P, HT, TOK], F32R)
        raw = sb("raw", [P, RING, UK, N])
        w_hi, w_lo = sb("w_hi", [P, RING, UK, N], F32R), sb("w_lo", [P, RING, UK, N], F32R)
        mix = sb("mix", [P, CT * (TOK + 3) + 7 * CT * TOK])
        fT, qT = sb("fT", [P, CT, TOK]), sb("qT", [P, CT, TOK])
        v_sb, silu = sb("v_sb", [P, TILES, N]), sb("silu", [P, TILES, N])
        zt, o_sb = sb("zt", [P, TILES, N]), sb("o_sb", [P, TILES, N])
        masks = sb("masks", [P, len(LEVELS), 64], BF16)
        ident = sb("ident", [P, P])
        sc = sb("sc", [P, 3, P])
        gates = sb("gates", [P, 504])
        pv = sb("pv", [P, 2, P])
        junk = sb("junk", [P, N], BF16)
        ssq, ms, rs = sb("ssq", [P, 5, TILES, XC]), sb("ms", [P, 5, TILES]), sb("rs", [P, 5, TILES])
        osq, oms, ors = (sb(n, [P, HEADS, TILES]) for n in ("osq", "oms", "ors"))
        mhalf = sb("mhalf", [P, 4])
        warm = sb("warm", [P, 1])
        lbs = sb("lbs", [P, 2, HEADS])
        lam = sb("lam", [P, 2, NB])
        t8 = sb("t8", [P, 7, NB])

        xbT = mix[:, 0:CT * (TOK + 3)].rearrange("p (b t) -> p b t", b=CT)
        part = [mix[:, CT * (TOK + 3) + i * CT * TOK:CT * (TOK + 3) + (i + 1) * CT * TOK] for i in range(7)]
        xc, rg, ig, aa, ww, geluT = *(part[i] for i in range(5)), part[5:7]
        wa_sb, wx_sb = qT[:, :, :].rearrange("p b t -> p (b t)"), fT[:, :, :].rearrange("p b t -> p (b t)")
        lev = [[mix[:, (8 * k + i) * 2 * TOK:(8 * k + i + 1) * 2 * TOK] for i in range(8)] for k in range(2)]
        qlev, klev = lev
        proj = mix[:, 0:TILES * D].rearrange("p (i d) -> p i d", i=TILES)
        ple_b, fin_g = mix[:, TILES * D:TILES * D + D], mix[:, TILES * D + D:TILES * D + 2 * D]
        p_sb = fT[:, 0:UK, :]
        PK = 20
        prm = zt[:, :, 0:P]

        acc = [ctx.enter_context(nc.psum_tensor(f"acc{i}", [P, TILES, N], F32)) for i in range(2)]
        tb = [ctx.enter_context(nc.psum_tensor(f"tb{i}", [P, UK, TOK], F32)) for i in range(2)]
        mm = ctx.enter_context(nc.psum_tensor("mm", [P, 2, N], F32))

        gain_in, params_in, x_in = sem("gain_in"), sem("params_in"), [sem(f"x_in{n}") for n in range(XC)]
        lru_w_in, late_in, out_done = sem("lru_w_in"), sem("late_in"), sem("out_done")
        raw_in = [sem(f"raw_in{s}") for s in range(RING)]
        hi_ready, lo_ready, unit_done = sem("hi_ready"), sem("lo_ready"), sem("unit_done")
        accs = Uses({"act": sem("acc_read_by_act"), "dve": sem("acc_read_by_dve")})
        turns = Uses({"act": sem("turn_read_by_act"), "dve": sem("turn_read_by_dve")})
        mids = Uses({"act": sem("mid_read_by_act"), "dve": sem("mid_read_by_dve")})
        turned, mid_done, turn_hi = sem("turned"), sem("mid_done"), sem("turn_hi")
        zeroed, consts = sem("zeroed"), sem("consts")
        exps_in, exps_out, lam_ready = sem("exps_in"), sem("exps_out"), sem("lam_ready")
        squared, ms_ready, rs_ready = sem("squared"), sem("ms_ready"), sem("rs_ready")
        conv_ready, ratio_ready, root_ready = sem("conv_ready"), sem("ratio_ready"), sem("root_ready")
        tanh_ready, decay_ready = sem("tanh_ready"), sem("decay_ready")
        lru_y, lru_hi, lru_out = sem("lru_y"), sem("lru_hi"), sem("lru_out")
        levels_ready = sem("levels_ready")
        oms_ready, ors_ready, gated = sem("oms_ready"), sem("ors_ready"), sem("gated")
        sig_ready, x_final, scaled = sem("sig_ready"), sem("x_final"), sem("scaled")
        last_done, last_pre = sem("last_done"), sem("last_pre")
        final_dve, final_act = sem("final_dve"), sem("final_act")
        own_dve, own_pool = sem("own_dve"), sem("own_pool")

        block = ctx.enter_context(nc.Block())

        X_LAST = {1: ("down", 0, 1), 2: ("out", 1), 3: ("down", 1, 1)}
        squares_made, squared_at = [0], {}
        X0_AFTER = {1: 1, 3: 2, 4: 3}
        hi_at = {}

        def wait_x_chunk(eng, nu, n):
            if nu == 0:
                eng.wait_ge(x_in[n], 16)
            elif nu == 4:
                eng.wait_ge(x_final, n + 1)
            else:
                eng.wait_ge(*accs.done(accs.at[(*X_LAST[nu], n)]))

        @block.tensor
        def _(pe):
            def wait_use(uses, index):
                if index >= 2:
                    pe.wait_ge(*uses.done(index - 2))

            def tile_products(slot, stat, kts, i, pair, first, last):
                hi, lo = stat
                o, col = acc[pair][:, i, :], slice(i * P, (i + 1) * P)
                for k, kt in enumerate(kts):
                    pe.matmul(o, hi[:, kt, col], w_hi[:, slot, k, :], start=first and k == 0, stop=False)
                    pe.matmul(o, hi[:, kt, col], w_lo[:, slot, k, :], start=False, stop=False)
                    m = pe.matmul(o, lo[:, kt, col], w_hi[:, slot, k, :], start=False, stop=last and k == UK - 1)
                return m

            def unit(u, slot, stat, kts, pair, first, last):
                pe.wait_ge(lo_ready, u + 1)
                for i in range(TILES):
                    m = tile_products(slot, stat, kts, i, pair, first, last)
                m.then_inc(unit_done, 1)

            XT, HH = (xt_hi, xt_lo), (h_hi, h_lo)

            def turn(index, pieces, free=None):
                if free is None:
                    wait_use(turns, index)
                else:
                    pe.wait_ge(*free)
                for dst, src in pieces:
                    t = pe.transpose(dst, src, ident[:, :])
                t.then_inc(turned, 1)

            def turn_x(nu, n):
                wait_x_chunk(pe, nu, n)
                for h in range(2):
                    index = turns.add(("x", nu, n, h), "dve")
                    turn(index, [(tb[index % 2][:, e, i * P:(i + 1) * P],
                                  x[:, i, (CT * n + 2 * h + e) * P:(CT * n + 2 * h + e + 1) * P])
                                 for e in range(2) for i in range(TILES)])

            def wait_x(nu, kt):
                pe.wait_ge(*turns.done(turns.at["x", nu, kt // CT, kt % CT // 2]))

            def ffn(f):
                for half in range(2):
                    c0, nch = CHUNK0[half], HALF[half]
                    up, down = ffn_unit(f, half)
                    for w, (key, reader) in enumerate((("ffn_gate", "act"), ("ffn_up", "dve"))):
                        wait_use(accs, accs.add((key, f, c0), reader))
                        for j in range(UD):
                            if half == 0 and w == 0:
                                wait_x(2 * f, UK * j)
                            u = up + w * UD + j
                            unit(u, u % RING, XT, range(UK * j, UK * j + UK), w, j == 0, j == UD - 1)
                            if half == 0 and f == 1 and w == 0 and j == 1:
                                turn_x(2, XC - 1)
                            if half == 0 and f == 0 and w == 0 and j < XC - 1:
                                turn_x(0, j + 1)
                            if half == 0 and f == 0 and w == 0 and j == XC:
                                pe.wait_ge(params_in, 16 * 10)
                                pe.wait_ge(*mids.done(mids.add(("params",), "dve") - 1))
                                pe.transpose(mm[:, 0, 0:4 * KT], prm[0:4 * KT, 0, :], ident[0:4 * KT, 0:4 * KT])
                                pe.transpose(mm[:, 1, 0:P], prm[:, 1, :], ident[:, :]).then_inc(mid_done, 1)
                    first_acc, first_turn = len(accs.readers), len(turns.readers)
                    for c in range(c0 + 1, c0 + nch):
                        accs.add(("ffn_gate", f, c), "act")
                        accs.add(("ffn_up", f, c), "dve")
                        for h in range(2):
                            turns.add(("a", f, c - 1, h), "dve")
                    with pe.Fori(0, nch - 1) as it:
                        for w in range(2):
                            s, v = accs.done(first_acc + w - 2)
                            pe.wait_ge(s, it + v)
                            for j in range(UD):
                                u = up + 2 * UD + w * UD + j
                                unit(it * (2 * UD) + u, u % RING, XT, range(UK * j, UK * j + UK), w,
                                     j == 0, j == UD - 1)
                                if w == 0 and j == 1:
                                    s, v = accs.done(accs.at["ffn_up", f, c0])
                                    pe.wait_ge(s, it + v)
                                    for h in range(2):
                                        s, v = turns.done(first_turn + h - 2)
                                        turn(first_turn + h,
                                             [(tb[(first_turn + h) % 2][:, e, i * P:(i + 1) * P],
                                               zt[:, i, (2 * h + e) * P:(2 * h + e + 1) * P])
                                              for e in range(2) for i in range(TILES)], free=(s, it * 2 + v))
                    for n in range(XC):
                        index = accs.add(("down", f, half, n), "dve")
                        wait_use(accs, index)
                        for j in range(DOWN[half]):
                            if n == 0 and j == 0:
                                pe.wait_ge(*turns.done(turns.at["a", f, c0 + nch - 2, 1]))
                            if n == 0 and j == DOWN[half] - 2:
                                pe.wait_ge(*turns.done(turns.at["a", f, c0 + nch - 1, 1]))
                            u = down + n * DOWN[half] + j
                            unit(u, u % RING, HH, range(UK * j, UK * j + UK), index % 2, j == 0,
                                 j == DOWN[half] - 1)
                            if j == 5 and f == 1 and half == 1 and n == 1:
                                pe.wait_ge(late_in, 48)
                                t = turns.add(("p",), "dve")
                                turn(t, [(tb[t % 2][:, e, i * P:(i + 1) * P],
                                          p_sb[:, i, e * P:(e + 1) * P])
                                         for e in range(2) for i in range(TILES)])
                            if j != 1:
                                continue
                            if n == 0:
                                pe.wait_ge(*accs.done(accs.at["ffn_up", f, c0 + nch - 1]))
                                for h in range(2):
                                    t = turns.add(("a", f, c0 + nch - 1, h), "dve")
                                    turn(t, [(tb[t % 2][:, e, i * P:(i + 1) * P],
                                              zt[:, i, (2 * h + e) * P:(2 * h + e + 1) * P])
                                             for e in range(2) for i in range(TILES)])
                            elif half == 1:
                                turn_x(2 * f + 1, n - 1)

            def lru_products(h, pair):
                index = mids.add(("lru", h, pair), "act")
                if h == 0 and pair == 0:
                    pe.wait_ge(lru_w_in, 32)
                pe.wait_ge(*mids.done(index - 1))
                pe.wait_ge(conv_ready, CT * h + 2 * pair + 2)
                for w, wt in enumerate((wa_sb, wx_sb)):
                    for e in range(2):
                        b = 2 * pair + e
                        m = pe.matmul(mm[:, w, e * TOK:(e + 1) * TOK],
                                      wt[:, (CT * h + b) * P:(CT * h + b + 1) * P],
                                      xc[:, b * TOK:(b + 1) * TOK], start=True, stop=True)
                m.then_inc(mid_done, 1)

            def scores(head):
                s, e = head // 2, head % 2
                pe.wait_ge(*mids.done(mids.add(("score", head), "dve") - 1))
                pe.wait_ge(levels_ready, s + 1)

                def part_of(level, i):
                    return level[:, (e * TILES + i) * P:(e * TILES + i + 1) * P]

                for i in range(TILES):
                    for n, L in enumerate(LEVELS):
                        upper = part_of(qlev[n], i).rearrange("p (n two l) -> p n two l", two=2, l=L)[:, :, 1, :]
                        to = mm[:, i, 64 * n:64 * n + 64].rearrange("p (n l) -> p n l", l=L)
                        m = pe.matmul(to, part_of(klev[n], i), upper, start=True, stop=True)
                m.then_inc(mid_done, 1)
                index = turns.add(("diag", head), "dve")
                wait_use(turns, index)
                bank = tb[index % 2][:, :, :].rearrange("p a b -> p (a b)")
                q = qT[:, head % CT, :]
                for i in range(TILES):
                    pe.matmul(bank[:, i * P:(i + 1) * P], part_of(klev[0], i), q[:, i * P:(i + 1) * P],
                              start=True, stop=True)
                pe.matmul(bank[:, 2 * P:3 * P], part_of(klev[7], 0), part_of(qlev[7], 1),
                          start=True, stop=True).then_inc(turned, 1)

            def outputs(head):
                index = turns.add(("o", head), "act")
                wait_use(turns, index)
                pe.wait_ge(*turns.done(turns.at["diag", head]))
                pe.wait_ge(*accs.done(accs.at["z", 6 + CT * (head // CT)]))
                bank, col = tb[index % 2], slice(head % CT * P, (head % CT + 1) * P)
                pe.matmul(bank[:, 0, 0:P], sc[:, 0, :], v_sb[:, 0, col], start=True, stop=True)
                pe.matmul(bank[:, 1, 0:P], sc[:, 2, :], v_sb[:, 0, col], start=True, stop=False)
                pe.matmul(bank[:, 1, 0:P], sc[:, 1, :], v_sb[:, 1, col], start=False,
                          stop=True).then_inc(turned, 1)

            def mixer_side(j):
                if j == 1:
                    turn_x(1, XC - 1)
                for h in range(2):
                    for pair in range(2):
                        if j == LRU0[h] + 5 + 4 * pair:
                            lru_products(h, pair)
                for ci in TURNED:
                    if j == UD * (ci + 1) + 1:
                        pe.wait_ge(*accs.done(accs.at["z", ci]))
                        for h in range(2):
                            t = turns.add((*Z[ci][:2], h), "dve" if Z[ci][0] == "f" else "act")
                            turn(t, [(tb[t % 2][:, e, i * P:(i + 1) * P],
                                      zt[:, i, (2 * h + e) * P:(2 * h + e + 1) * P])
                                     for e in range(2) for i in range(TILES)])
                for head in range(HEADS):
                    if j == O_AT[head]:
                        outputs(head)
                for head in range(HEADS):
                    if j == SCORE[head]:
                        scores(head)
                for s in range(HEADS // 2):
                    if j == Y_AT[s]:
                        pe.wait_ge(gated, s + 1)
                        t = turns.add(("y", s), "dve")
                        turn(t, [(tb[t % 2][:, e, i * P:(i + 1) * P],
                                  o_sb[:, i, ((2 * s + e) % CT) * P:((2 * s + e) % CT + 1) * P])
                                 for e in range(2) for i in range(TILES)])
                for n in range(XC - 1):
                    if j == U_OUT[1] - U_IN + 2 * n + 3:
                        turn_x(2, n)

            pe.wait_ge(consts, 1)
            pe.wait_ge(gain_in, 16)
            mids.add(("gain",), "dve")
            pe.transpose(mm[:, 0, 0:KT], prm[0:KT, 0, :], ident[0:KT, 0:KT]).then_inc(mid_done, 1)
            turn_x(0, 0)
            ffn(0)
            for ci in range(len(Z)):
                index = accs.add(("z", ci), "act")
                wait_use(accs, index)
                for k in range(UD):
                    if ci == 0:
                        wait_x(1, UK * k)
                    j = UD * ci + k
                    unit(U_IN + j, j % RING, XT, range(UK * k, UK * k + UK), index % 2, k == 0, k == UD - 1)
                    mixer_side(j)
            for o in range(2):
                for n in range(XC):
                    index = accs.add(("out", o, n), "dve")
                    wait_use(accs, index)
                    for k in range(OUT[o]):
                        if n == 0 and o == 0 and k == 0:
                            pe.wait_ge(lru_out, 2)
                            pe.wait_ge(*turns.done(turns.at["y", 1]))
                        if n == 0 and o == 1 and k == 0:
                            pe.wait_ge(*turns.done(turns.at["y", 3]))
                        j = U_OUT[o] - U_IN + n * OUT[o] + k
                        unit(U_IN + j, j % RING, HH, OUT_KT[o][UK * k:UK * k + UK], index % 2, k == 0,
                             k == OUT[o] - 1)
                        mixer_side(j)
            ffn(1)
            for n in range(XC):
                index = accs.add(("proj", n), "act")
                wait_use(accs, index)
                if n == 0:
                    pe.wait_ge(*turns.done(turns.at["p",]))
                unit(U_PROJ + n, n % RING, HH, (PK, PK + 1), index % 2, True, True)
                if n == 1:
                    turn_x(3, XC - 1)
            for n in range(XC):
                index = accs.add(("ple", n), "dve")
                wait_use(accs, index)
                for k in range(UD if n < XC - 1 else UD - RING):
                    if n == 0:
                        wait_x(3, UK * k)
                    u = U_GATE + n * UD + k
                    unit(u, u % RING, XT, range(UK * k, UK * k + UK), index % 2, k == 0, k == UD - 1)
            for i in range(TILES):
                for k in range(UD - RING, UD):
                    u = U_GATE + (XC - 1) * UD + k
                    if i == 0:
                        pe.wait_ge(lo_ready, u + 1)
                    m = tile_products(u % RING, XT, range(UK * k, UK * k + UK), i, index % 2, False, k == UD - 1)
                m.then_inc(last_done, 1)

        @block.sync
        def _(sp):
            def load(u, slot, w, row, col):
                if isinstance(u, int) and u < RING:
                    return
                sp.wait_ge(lo_ready, u - (RING - 1))
                src = w[row * P:(row + UK) * P, bass.ds(col, N)].rearrange("(k p) n -> p k n", p=P)
                sp.dma_start(raw[:, slot, :, :], src).then_inc(raw_in[slot], 16)

            def load_ffn(f):
                w_gate, w_up, w_down = ffn_w[f]
                for half in range(2):
                    up, down = ffn_unit(f, half)
                    for w, wt in enumerate((w_gate, w_up)):
                        for j in range(UD):
                            load(up + w * UD + j, j % RING, wt, UK * j, CHUNK0[half] * N)
                    with sp.Fori(0, HALF[half] - 1) as it:
                        for w, wt in enumerate((w_gate, w_up)):
                            for j in range(UD):
                                load(it * (2 * UD) + (up + 2 * UD + w * UD + j), j % RING, wt, UK * j,
                                     it * N + (CHUNK0[half] + 1) * N)
                    for n in range(XC):
                        for j in range(DOWN[half]):
                            u = down + n * DOWN[half] + j
                            load(u, u % RING, w_down, CHUNK0[half] * CT + UK * j, n * N)

            first_units = ffn_w[0][0][:, 0:N].rearrange("(u k p) n -> u p k n", k=UK, p=P)
            for n in range(XC):
                sp.dma_start(x[:, :, n * N:(n + 1) * N], x_dram[:, :, n * N:(n + 1) * N]).then_inc(x_in[n], 16)
                sp.dma_start(raw[:, n, :, :], first_units[n]).then_inc(raw_in[n], 16)
            for k, (name, i, row) in enumerate((
                    ("mix_norm", 0, 16), ("ffn2_norm", 0, 32), ("ple_norm", 0, 48),
                    ("hgrn_lower_bounds", 1, 0), ("conv_b", 1, 48), ("lru_b_a", 1, 56), ("lru_b_x", 1, 64),
                    ("lru_lambda", 1, 72))):
                src = A[name].rearrange("a (r c) -> (a r) c", c=P)
                if (i, row) == (1, 0):
                    sp.wait_ge(zeroed, 1)
                sp.dma_start(prm[row:row + src.shape[0], i, :], src).then_inc(params_in, 16)
            src = A["conv_w"].rearrange("l k (r c) -> (l k r) c", c=P)
            sp.dma_start(prm[16:16 + src.shape[0], 1, :], src).then_inc(params_in, 16)
            sp.dma_start(prm[80:81, 1, :], A["hgrn_g_norm"]).then_inc(params_in, 16)
            load_ffn(0)
            for ci, (_, _, col) in enumerate(Z):
                for k in range(UD):
                    load(U_IN + UD * ci + k, k % RING, w_in, UK * k, col)
            for o in range(2):
                for n in range(XC):
                    for k in range(OUT[o]):
                        u = U_OUT[o] + n * OUT[o] + k
                        load(u, u % RING, w_out, OUT_KT[o][UK * k], n * N)
            load_ffn(1)
            for n in range(XC):
                load(U_PROJ + n, n % RING, w_proj, 0, n * N)
            for n in range(XC):
                for k in range(UD):
                    load(U_GATE + n * UD + k, k % RING, w_ple, UK * k, n * N)
            for i in range(TILES):
                for ready, half in ((final_dve, 0), (final_act, 1)):
                    part_x = slice(half * D // 2, (half + 1) * D // 2)
                    sp.wait_ge(ready, i + 1)
                    sp.dma_start(out_dram[:, i, part_x], proj[:, i, part_x]).then_inc(out_done, 16)
            sp.wait_ge(out_done, 16 * TILES * 2)

        @block.scalar
        def _(act):
            def round_hi(u, slot, landed):
                act.wait_ge(raw_in[slot], landed * 16 + 16)
                if not (isinstance(u, int) and u < RING):
                    act.wait_ge(unit_done, u - (RING - 1))
                act.activation(w_hi[:, slot, :, :], raw[:, slot, :, :], ACT.Copy).then_inc(hi_ready, 1)

            def bank_of(key):
                act.wait_ge(turned, turns.at[key] + 1)
                return tb[turns.at[key] % 2]

            def count_hi(key, ins):
                hi_at[key] = len(hi_at) + 1
                if ins is not None:
                    ins.then_inc(turn_hi, 1)

            def x_hi(nu, n):
                for h in range(2):
                    bank = bank_of(("x", nu, n, h))
                    for e in range(2):
                        kt = CT * n + 2 * h + e
                        ins = act.activation(xt_hi[:, kt, :], bank[:, e, :], ACT.Copy,
                                             scale=pv[:, 0, KT * nu + kt:KT * nu + kt + 1])
                    count_hi(("x", nu, n, h), ins)

            def square(src, total):
                if squares_made[0]:
                    act.wait_ge(squared, squares_made[0])
                act.activation(junk[:, 0:src.shape[-1]], src, ACT.Square, accum_out=total).then_inc(squared, 1)
                squares_made[0] += 1

            def squares(nu, n):
                wait_x_chunk(act, nu, n)
                for i in range(TILES):
                    square(x[:, i, n * N:(n + 1) * N], ssq[:, nu, i, n:n + 1])
                squared_at[nu] = squares_made[0]

            def silu_gate(f):
                for i in range(TILES):
                    ins = act.activation(silu[:, i, :], acc[0][:, i, :], ACT.Silu, scale=rs[:, 2 * f, i:i + 1])
                ins.then_inc(accs.read["act"], 1)

            def ffn(f):
                for half in range(2):
                    c0, nch = CHUNK0[half], HALF[half]
                    up, down = ffn_unit(f, half)
                    for j in range(2 * UD):
                        round_hi(up + j, j % RING, (up + j) // RING)
                        if half == 0 and f == 1:
                            if j == 0:
                                squares(2, 2)
                                x_hi(2, 1)
                            if j == 2:
                                squares(2, 3)
                                x_hi(2, 2)
                            if j == 4:
                                x_hi(2, 3)
                        if half == 0 and f == 0:
                            if j in X0_AFTER:
                                x_hi(0, X0_AFTER[j])
                            if XC < j <= 2 * XC:
                                squares(0, j - XC - 1)
                            if j == 9:
                                act.wait_ge(exps_in, 1)
                                act.activation(t8[:, 0:3, :], t8[:, 0:3, :], ACT.Exp).then_inc(exps_out, 1)
                        if j == 10:
                            if half == 0:
                                act.wait_ge(rs_ready, 2 * f + 1)
                            act.wait_ge(unit_done, up + UD)
                            silu_gate(f)
                    t0, up0 = turns.at["a", f, c0, 0], accs.at["ffn_up", f, c0]
                    for c in range(c0 + 1, c0 + nch):
                        for h in range(2):
                            count_hi(("a", f, c - 1, h), None)
                    with act.Fori(0, nch - 1) as it:
                        for j in range(2 * UD):
                            u = up + 2 * UD + j
                            round_hi(it * (2 * UD) + u, j % RING, it * (2 * UD // RING) + u // RING)
                            if j == 4:
                                for h in range(2):
                                    act.wait_ge(turned, it * 2 + (t0 + h + 1))
                                    act.activation(h_hi[:, bass.ds(it * CT + 2 * h, 2), :],
                                                   tb[(t0 + h) % 2][:, :, :], ACT.Copy).then_inc(turn_hi, 1)
                            if j == 10:
                                act.wait_ge(unit_done, it * (2 * UD) + (up + 3 * UD))
                                s, v = accs.done(up0)
                                act.wait_ge(s, it + v)
                                silu_gate(f)
                    for n in range(XC):
                        for j in range(DOWN[half]):
                            u = down + n * DOWN[half] + j
                            round_hi(u, u % RING, u // RING)
                            if j == 2 and half == 1 and n >= 1:
                                squares(2 * f + 1, n - 1)
                            if j == 4 and n == 0:
                                for h in range(2):
                                    key = ("a", f, c0 + nch - 1, h)
                                    kt = CT * (nch - 1) + 2 * h
                                    count_hi(key, act.activation(h_hi[:, kt:kt + 2, :], bank_of(key)[:, :, :],
                                                                 ACT.Copy))
                            if j == 4 and half == 1 and n >= 1:
                                x_hi(2 * f + 1, n - 1)
                            if j == 8 and half == 1 and f == 1 and n == 1:
                                count_hi(("p",), act.activation(h_hi[:, PK:PK + 2, :], bank_of(("p",))[:, :, :],
                                                                ACT.Copy))

            def leave(ci):
                kind, g, _ = Z[ci]
                act.wait_ge(unit_done, U_IN + UD * (ci + 1))
                if ci == 0:
                    act.wait_ge(rs_ready, 2)
                dst = {"v": v_sb, "g": silu}.get(kind, zt)
                fn = {"gate": ACT.Gelu_apprx_tanh, "f": ACT.Sigmoid, "g": ACT.Silu}.get(kind, ACT.Copy)
                pair = acc[accs.at["z", ci] % 2]
                for i in range(TILES):
                    ins = act.activation(dst[:, i, :], pair[:, i, :], fn, scale=rs[:, 1, i:i + 1])
                ins.then_inc(accs.read["act"], 1)

            def copy_turned(kind, g):
                for h in range(2):
                    bank = bank_of((kind, g, h))
                    if kind == "xb":
                        if g == 1 and h == 0:
                            act.wait_ge(conv_ready, CT)
                        dst = xbT[:, 2 * h:2 * h + 2, 3:3 + TOK]
                    elif kind == "gate":
                        dst = geluT[g].rearrange("p (b t) -> p b t", b=CT)[:, 2 * h:2 * h + 2, :]
                    else:
                        dst = qT[:, 2 * h:2 * h + 2, :]
                        act.wait_ge(mid_done, mids.at["lru", 1, 1] + 1)
                    act.activation(dst, bank[:, :, :], ACT.Copy).then_inc(turns.read["act"], 1)

            def lru_sigmoids(h, pair):
                act.wait_ge(mid_done, mids.at["lru", h, pair] + 1)
                if h == 1 and pair == 0:
                    act.wait_ge(lru_out, 1)
                for w, (dst, bias0) in enumerate(((rg, 56), (ig, 64))):
                    for e in range(2):
                        b = 2 * pair + e
                        k = bias0 + CT * h + b
                        ins = act.activation(dst[:, b * TOK:(b + 1) * TOK], mm[:, w, e * TOK:(e + 1) * TOK],
                                             ACT.Sigmoid, bias=pv[:, 1, k:k + 1])
                ins.then_inc(mids.read["act"], 1)

            def lru_gate(h, dst, fn, k, done):
                act.wait_ge(*mids.done(mids.at["lru", h, 1]))
                act.wait_ge(lam_ready, 1)
                for b in range(CT):
                    ins = act.activation(dst[:, b * TOK:(b + 1) * TOK], rg[:, b * TOK:(b + 1) * TOK], fn,
                                         scale=lam[:, k, CT * h + b:CT * h + b + 1])
                ins.then_inc(done, 1)

            def copy_o(head):
                bank = bank_of(("o", head))
                for i in range(TILES):
                    square(bank[:, i, 0:P], osq[:, head, i:i + 1])
                squared_at["o", head] = squares_made[0]
                hh = head % CT
                act.activation(o_sb[:, :, hh * P:(hh + 1) * P], bank[:, :, 0:P], ACT.Copy)\
                   .then_inc(turns.read["act"], 1)

            def mixer_side(j):
                if j == 2:
                    squares(1, 3)
                if j == 4:
                    x_hi(1, 3)
                for ci, (kind, g, _) in enumerate(Z):
                    if j == UD * (ci + 1) + 2:
                        leave(ci)
                    if j == UD * (ci + 1) + 4 and kind in ("gate", "xb", "q"):
                        copy_turned(kind, g)
                for h in range(2):
                    b = LRU0[h]
                    if j in (b + 8, b + 12):
                        lru_sigmoids(h, (j - b - 8) // 4)
                    if j == b + 13:
                        lru_gate(h, ww, ACT.Tanh, 1, tanh_ready)
                    if j == b + 14:
                        lru_gate(h, aa, ACT.Exp, 0, decay_ready)
                    if j == b + 17:
                        act.wait_ge(ratio_ready, h + 1)
                        act.activation(ww, ww, ACT.Sqrt).then_inc(root_ready, 1)
                    if j == b + 22:
                        act.wait_ge(lru_y, h + 1)
                        dst = h_hi[:, HEADS + CT * h:HEADS + CT * h + CT, :].rearrange("p b t -> p (b t)")
                        act.activation(dst, rg, ACT.Copy).then_inc(lru_hi, 1)
                for head in range(HEADS):
                    if j == O_AT[head] + 3:
                        copy_o(head)
                for s in range(HEADS // 2):
                    if j == Y_AT[s] + 3:
                        count_hi(("y", s), act.activation(h_hi[:, 2 * s:2 * s + 2, :], bank_of(("y", s))[:, :, :],
                                                          ACT.Copy, scale=pv[:, 1, 80:81]))
                if j == U_OUT[1] - U_IN + 4:
                    squares(2, 0)
                if j == U_OUT[1] - U_IN + 6:
                    squares(2, 1)
                    x_hi(2, 0)

            act.dma_start(prm[0:KT, 0, :], A["ffn1_norm"].rearrange("a (r c) -> (a r) c", c=P)).then_inc(gain_in, 16)
            act.wait_ge(consts, 1)
            act.activation(warm[:, :], mhalf[:, 0:1], ACT.Copy)
            act.wait_ge(*mids.done(mids.at["gain",]))
            x_hi(0, 0)
            ffn(0)
            for j in range(MIX):
                round_hi(U_IN + j, j % RING, (U_IN + j) // RING)
                mixer_side(j)
            ffn(1)
            for j in range(XC + UD * XC):
                u = U_PROJ + j
                round_hi(u, u % RING, u // RING)
                if j == 2:
                    squares(3, 3)
                if j == 4:
                    x_hi(3, 3)
                if 3 <= j < 3 + XC:
                    n = j - 3
                    act.wait_ge(unit_done, U_PROJ + n + 1)
                    act.activation(proj[:, :, n * N:(n + 1) * N], acc[accs.at["proj", n] % 2][:, :, :],
                                   ACT.Copy).then_inc(accs.read["act"], 1)
                for n in range(XC - 1):
                    if j == XC + UD * n + 11:
                        act.wait_ge(*accs.done(accs.at["ple", n]))
                        act.activation(zt[:, :, :], zt[:, :, :], ACT.Sigmoid).then_inc(sig_ready, 1)
                    if j == XC + UD * n + 13:
                        squares(4, n)
            for i in range(TILES):
                act.wait_ge(last_pre, i + 1)
                act.activation(zt[:, i, :], zt[:, i, :], ACT.Sigmoid).then_inc(sig_ready, 1)
                act.wait_ge(x_final, XC + i)
                square(x[:, i, D - N:D], ssq[:, 4, i, XC - 1:XC])
                squared_at["final", i] = squares_made[0]
                act.wait_ge(rs_ready, 5 + i)
                act.wait_ge(scaled, i + 1)
                act.activation(proj[:, i, D // 2:D], proj[:, i, D // 2:D], ACT.Copy, scale=rs[:, 4, i:i + 1])\
                   .then_inc(final_act, 1)

        @block.vector
        def _(dve):
            chain = [0]

            def link(ins):
                ins.then_inc(own_dve, 1)
                chain[0] += 1
                dve.wait_ge(own_dve, chain[0])

            def split(u, slot):
                dve.wait_ge(hi_ready, u + 1)
                dve.tensor_tensor(w_lo[:, slot, :, :], raw[:, slot, :, :], w_hi[:, slot, :, :].bitcast(F32),
                                  ALU.subtract).then_inc(lo_ready, 1)

            def bank_hi(key):
                dve.wait_ge(turn_hi, hi_at[key])
                return tb[turns.at[key] % 2]

            def x_lo(nu, n):
                for h in range(2):
                    bank = bank_hi(("x", nu, n, h))
                    for e in range(2):
                        kt = CT * n + 2 * h + e
                        ins = dve.scalar_tensor_tensor(
                            out=xt_lo[:, kt, :], in0=bank[:, e, :], scalar=pv[:, 0, KT * nu + kt:KT * nu + kt + 1],
                            in1=xt_hi[:, kt, :].bitcast(F32), op0=ALU.mult, op1=ALU.subtract)
                    ins.then_inc(turns.read["dve"], 1)

            def h_lo_of(key, kt):
                dve.tensor_tensor(h_lo[:, kt:kt + 2, :], bank_hi(key)[:, :, :], h_hi[:, kt:kt + 2, :].bitcast(F32),
                                  ALU.subtract).then_inc(turns.read["dve"], 1)

            def row_factors(nu):
                dve.wait_ge(squared, squared_at[nu])
                link(dve.tensor_reduce(ms[:, nu, :], ssq[:, nu, :, :], AX.X, ALU.add))
                dve.tensor_scalar(ms[:, nu, :], ms[:, nu, :], 1.0 / D, EPS, ALU.mult, ALU.add).then_inc(ms_ready, 1)

            def hidden(f):
                for i in range(TILES):
                    ins = dve.scalar_tensor_tensor(out=zt[:, i, :], in0=acc[1][:, i, :],
                                                   scalar=rs[:, 2 * f, i:i + 1], in1=silu[:, i, :],
                                                   op0=ALU.mult, op1=ALU.mult)
                ins.then_inc(accs.read["dve"], 1)

            def add_to_x(key, unit, n, factor):
                dve.wait_ge(unit_done, unit)
                pair = acc[accs.at[key] % 2]
                for i in range(TILES):
                    xn = x[:, i, n * N:(n + 1) * N]
                    ins = dve.scalar_tensor_tensor(out=xn, in0=pair[:, i, :], scalar=factor, in1=xn,
                                                   op0=ALU.mult, op1=ALU.add)
                ins.then_inc(accs.read["dve"], 1)

            def down_to_x(f, half, n):
                down = ffn_unit(f, half)[1]
                add_to_x(("down", f, half, n), down + DOWN[half] * (n + 1), n, 0.5)

            def out_to_x(o, n):
                add_to_x(("out", o, n), U_OUT[o] + OUT[o] * (n + 1), n, 1.0)

            a0, a1, lm = pv[:, 1, 0:HEADS], pv[:, 1, HEADS:2 * HEADS], pv[:, 1, 72:72 + NB]
            t = [t8[:, i, :] for i in range(7)]

            def exponents():
                dve.wait_ge(mid_done, mids.at["params",] + 1)
                dve.tensor_copy(pv[:, 0, KT:4 * KT], mm[:, 0, KT:4 * KT])
                dve.tensor_copy(pv[:, 1, :], mm[:, 1, 0:P]).then_inc(mids.read["dve"], 1)
                dve.wait_ge(*mids.done(mids.at["params",]))
                link(dve.tensor_tensor(t[3], a0, a1, ALU.max))
                dve.tensor_tensor(t[0], a0, t[3], ALU.subtract)
                dve.tensor_tensor(t[1], a1, t[3], ALU.subtract)
                dve.scalar_tensor_tensor(out=t[2], in0=lm, scalar=-1.0, in1=lm, op0=ALU.mult,
                                         op1=ALU.min).then_inc(exps_in, 1)

            def lower_bounds():
                dve.wait_ge(exps_out, 1)
                link(dve.tensor_tensor(t[3], t[0], t[1], ALU.add))
                link(dve.reciprocal(t[3], t[3]))
                link(dve.tensor_tensor(lbs[:, 0, :], t[0], t[3], ALU.mult))
                link(dve.tensor_scalar(lbs[:, 1, :], lbs[:, 0, :], -1.0, 1.0, ALU.mult, ALU.add))

            def softplus():
                link(dve.tensor_scalar(t[4], t[2], 2.0, None, ALU.add))
                link(dve.reciprocal(t[4], t[4]))
                link(dve.tensor_tensor(t[4], t[2], t[4], ALU.mult))
                link(dve.tensor_tensor(t[5], t[4], t[4], ALU.mult))
                link(dve.tensor_scalar(t[6], t[5], 1.0 / SERIES[0], None, ALU.mult))
                for c in SERIES[1:]:
                    link(dve.scalar_tensor_tensor(out=t[6], in0=t[6], scalar=1.0 / c, in1=t[5], op0=ALU.add,
                                                  op1=ALU.mult))
                link(dve.scalar_tensor_tensor(out=t[6], in0=t[6], scalar=1.0, in1=t[4], op0=ALU.add, op1=ALU.mult))
                link(dve.tensor_scalar(t[0], lm, -1.0, 0.0, ALU.mult, ALU.max))
                link(dve.scalar_tensor_tensor(out=t[1], in0=t[6], scalar=2.0, in1=t[0], op0=ALU.mult, op1=ALU.add))
                dve.tensor_scalar(lam[:, 0, :], t[1], -8.0, None, ALU.mult)
                dve.tensor_scalar(lam[:, 1, :], t[1], 8.0, None, ALU.mult).then_inc(lam_ready, 1)

            def ffn(f):
                for half in range(2):
                    c0, nch = CHUNK0[half], HALF[half]
                    up, down = ffn_unit(f, half)
                    for j in range(2 * UD):
                        split(up + j, j % RING)
                        if half == 0 and f == 0:
                            if j in X0_AFTER:
                                x_lo(0, X0_AFTER[j])
                            if j == 9:
                                row_factors(0)
                                exponents()
                            if j == 11:
                                lower_bounds()
                            if j == 13:
                                softplus()
                        if half == 0 and f == 1:
                            if j == 0:
                                out_to_x(1, 2)
                                x_lo(2, 1)
                            if j == 2:
                                out_to_x(1, 3)
                                x_lo(2, 2)
                            if j == 4:
                                x_lo(2, 3)
                            if j == 5:
                                row_factors(2)
                        if half == 1 and j == 2:
                            down_to_x(f, 0, XC - 1)
                    if half == 0:
                        dve.wait_ge(rs_ready, 2 * f + 1)
                    first, gate0 = hi_at["a", f, c0, 0], accs.at["ffn_gate", f, c0]
                    t0 = turns.at["a", f, c0, 0]
                    with dve.Fori(0, nch - 1) as it:
                        for j in range(2 * UD):
                            split(it * (2 * UD) + (up + 2 * UD + j), j % RING)
                            if j == 2:
                                dve.wait_ge(unit_done, it * (2 * UD) + (up + 2 * UD))
                                s, v = accs.done(gate0)
                                dve.wait_ge(s, it + v)
                                hidden(f)
                            if j == 4:
                                for h in range(2):
                                    dve.wait_ge(turn_hi, it * 2 + (first + h))
                                    hi = h_hi[:, bass.ds(it * CT + 2 * h, 2), :].bitcast(F32)
                                    dve.tensor_tensor(h_lo[:, bass.ds(it * CT + 2 * h, 2), :],
                                                      tb[(t0 + h) % 2][:, :, :], hi,
                                                      ALU.subtract).then_inc(turns.read["dve"], 1)
                    c = c0 + nch - 1
                    for n in range(XC):
                        for j in range(DOWN[half]):
                            u = down + n * DOWN[half] + j
                            split(u, u % RING)
                            if j == 2 and n == 0:
                                dve.wait_ge(unit_done, down)
                                dve.wait_ge(*accs.done(accs.at["ffn_gate", f, c]))
                                hidden(f)
                            if j == 2 and n >= 1:
                                down_to_x(f, half, n - 1)
                            if j == 4 and n == 0:
                                for h in range(2):
                                    h_lo_of(("a", f, c, h), CT * (nch - 1) + 2 * h)
                            if j == 4 and half == 1 and n >= 1:
                                x_lo(2 * f + 1, n - 1)
                            if j == 8 and half == 1 and f == 1 and n == 1:
                                h_lo_of(("p",), PK)

            def conv(h, b):
                if b == 0:
                    dve.wait_ge(*turns.done(turns.at["xb", h, 1]))
                    if h:
                        dve.wait_ge(lru_y, h)
                k = CT * h + b
                y = xc[:, b * TOK:(b + 1) * TOK]

                def tap(t):
                    return pv[:, 1, 16 + NB * t + k:17 + NB * t + k]

                link(dve.tensor_scalar(y, xbT[:, b, 3:3 + TOK], tap(CONV - 1), pv[:, 1, 48 + k:49 + k],
                                       ALU.mult, ALU.add))
                for t in range(CONV - 2, -1, -1):
                    ins = dve.scalar_tensor_tensor(out=y, in0=xbT[:, b, t:t + TOK], scalar=tap(t), in1=y,
                                                   op0=ALU.mult, op1=ALU.add)
                    if t:
                        link(ins)
                ins.then_inc(conv_ready, 1)

            def forget(g, h):
                dve.wait_ge(turned, turns.at["f", g, h] + 1)
                dve.wait_ge(mid_done, mids.at["lru", 1, 1] + 1)
                bank = tb[turns.at["f", g, h] % 2]
                for e in range(2):
                    head = CT * g + 2 * h + e
                    ins = dve.tensor_scalar(fT[:, 2 * h + e, :], bank[:, e, :], lbs[:, 1, head:head + 1],
                                            lbs[:, 0, head:head + 1], ALU.mult, ALU.add)
                ins.then_inc(turns.read["dve"], 1)

            GATE0 = {1: None}
            at = 0
            for L in LEVELS[1:]:
                GATE0[L] = at
                at += 2 * TOK // L

            def block_products(f2, L):
                return f2 if L == 1 else gates[:, GATE0[L]:GATE0[L] + 2 * TOK // L]

            def double(dst, src, prod, L, upper):
                d, s = (a.rearrange("p (n two l) -> p n two l", two=2, l=L) for a in (dst, src))
                by = prod.rearrange("p (n two) -> p n two", two=2)[:, :, 0 if upper else 1]
                by = by.unsqueeze(2).to_broadcast([P, TOK // L, L])
                k = 1 if upper else 0
                dve.tensor_tensor(d[:, :, k, :], s[:, :, k, :], by, ALU.mult)
                link(dve.tensor_copy(d[:, :, 1 - k, :], s[:, :, 1 - k, :]))

            def key_levels(s, piece):
                f2 = fT[:, 2 * (s % 2):2 * (s % 2) + 2, :].rearrange("p b t -> p (b t)")
                if piece == 0:
                    if s:
                        dve.wait_ge(turned, turns.at["diag", 2 * s - 1] + 1)
                    link(dve.tensor_scalar(klev[0], f2, -1.0, 1.0, ALU.mult, ALU.add))
                for n in range(2 * piece, min(2 * piece + 2, 7)):
                    L = LEVELS[n]
                    if n:
                        half = block_products(f2, L // 2).rearrange("p (n two) -> p n two", two=2)
                        link(dve.tensor_tensor(block_products(f2, L), half[:, :, 0], half[:, :, 1], ALU.mult))
                    double(klev[n + 1], klev[n], block_products(f2, L), L, False)

            def query_levels(s, piece):
                f2 = fT[:, 2 * (s % 2):2 * (s % 2) + 2, :].rearrange("p b t -> p (b t)")
                if piece == 0:
                    dve.wait_ge(*turns.done(turns.at["q", s // 2, s % 2]))
                    link(dve.tensor_tensor(qlev[0], qT[:, 2 * (s % 2):2 * (s % 2) + 2, :].rearrange("p b t -> p (b t)"),
                                           f2, ALU.mult))
                for n in range(2 * piece, min(2 * piece + 2, 7)):
                    double(qlev[n + 1], qlev[n], block_products(f2, LEVELS[n]), LEVELS[n], True)
                if piece == 3:
                    dve.sem_inc(levels_ready, 1)

            def keep_scores(head):
                dve.wait_ge(mid_done, mids.at["score", head] + 1)
                if head:
                    dve.wait_ge(turned, turns.at["o", head - 1] + 1)
                for n, L in enumerate(LEVELS):
                    dst = sc[:, 0:TILES, :].rearrange("p i (n two l) -> p i n two l", two=2, l=L)
                    for i in range(TILES):
                        ins = dve.copy_predicated(
                            dst[:, i, :, 1, :],
                            masks[:, n, :].bitcast(I16).rearrange("p (n l) -> p n l", l=L),
                            mm[:, i, 64 * n:64 * n + 64].rearrange("p (n l) -> p n l", l=L))
                    if L < LEVELS[-1]:
                        link(ins)
                ins.then_inc(mids.read["dve"], 1)
                dve.wait_ge(*mids.done(mids.at["score", head]))
                dve.wait_ge(turned, turns.at["diag", head] + 1)
                bank = tb[turns.at["diag", head] % 2][:, :, :].rearrange("p a b -> p (a b)")
                dve.tensor_copy(sc[:, 2, :], bank[:, 2 * P:3 * P])
                for i in range(TILES):
                    ins = dve.copy_predicated(sc[:, i, :], ident[:, :].bitcast(I32), bank[:, i * P:(i + 1) * P])
                ins.then_inc(turns.read["dve"], 1)

            def gate_o(s):
                dve.wait_ge(ors_ready, s + 1)
                dve.wait_ge(*turns.done(turns.at["o", 2 * s + 1]))
                dve.wait_ge(*accs.done(accs.at["z", 7 + CT * (s // 2)]))
                for e in range(2):
                    for i in range(TILES):
                        head, col = 2 * s + e, slice((2 * s + e) % CT * P, ((2 * s + e) % CT + 1) * P)
                        ins = dve.scalar_tensor_tensor(out=o_sb[:, i, col], in0=o_sb[:, i, col],
                                                       scalar=ors[:, head, i:i + 1], in1=silu[:, i, col],
                                                       op0=ALU.mult, op1=ALU.mult)
                ins.then_inc(gated, 1)

            def mixer_side(j):
                if j == 2:
                    down_to_x(0, 1, XC - 1)
                if j == 4:
                    x_lo(1, XC - 1)
                if j == 5:
                    row_factors(1)
                for h in range(2):
                    k = j - LRU0[h]
                    if 5 <= k < 5 + CT:
                        conv(h, k - 5)
                    if k == 13:
                        dve.wait_ge(*mids.done(mids.at["lru", h, 1]))
                        link(dve.tensor_tensor(ig, ig, xc, ALU.mult))
                    if k == 15:
                        dve.wait_ge(decay_ready, h + 1)
                        link(dve.tensor_tensor(xc, aa, aa, ALU.mult))
                    if k == 16:
                        dve.wait_ge(tanh_ready, h + 1)
                        dve.scalar_tensor_tensor(out=ww, in0=xc, scalar=1.0, in1=ww, op0=ALU.add,
                                                 op1=ALU.mult).then_inc(ratio_ready, 1)
                    if k == 18:
                        dve.wait_ge(root_ready, h + 1)
                        link(dve.tensor_tensor(ww, ww, ig, ALU.mult))
                    if k in (19, 20):
                        for b in range(2 * (k - 19), 2 * (k - 19) + 2):
                            part_b = slice(b * TOK, (b + 1) * TOK)
                            ins = dve.tensor_tensor_scan(xc[:, part_b], aa[:, part_b], ww[:, part_b], 0.0,
                                                         ALU.mult, ALU.add)
                        link(ins)
                    if k == 21:
                        dve.wait_ge(*turns.done(turns.at["gate", h, 1]))
                        dve.tensor_tensor(rg, xc, geluT[h], ALU.mult).then_inc(lru_y, 1)
                    if k == 22:
                        dve.wait_ge(lru_hi, h + 1)
                        blocks = slice(HEADS + CT * h, HEADS + CT * h + CT)
                        dve.tensor_tensor(h_lo[:, blocks, :].rearrange("p b t -> p (b t)"), rg,
                                          h_hi[:, blocks, :].bitcast(F32).rearrange("p b t -> p (b t)"),
                                          ALU.subtract).then_inc(lru_out, 1)
                for ci, (kind, g, _) in enumerate(Z):
                    for h in range(2):
                        if kind == "f" and j == UD * (ci + 1) + 4:
                            forget(g, h)
                for s in range(HEADS // 2):
                    if 0 <= j - B_AT[s] < 4:
                        key_levels(s, j - B_AT[s])
                    if 0 <= j - A_AT[s] < 4:
                        query_levels(s, j - A_AT[s])
                    if j == GATED_AT[s] - 1:
                        dve.wait_ge(squared, squared_at["o", 2 * s + 1])
                        dve.tensor_scalar(oms[:, 2 * s:2 * s + 2, :], osq[:, 2 * s:2 * s + 2, :], 1.0 / P, EPS,
                                          ALU.mult, ALU.add).then_inc(oms_ready, 1)
                    if j == GATED_AT[s]:
                        gate_o(s)
                    if j == Y_AT[s] + 3:
                        dve.scalar_tensor_tensor(
                            out=h_lo[:, 2 * s:2 * s + 2, :], in0=bank_hi(("y", s))[:, :, :], scalar=pv[:, 1, 80:81],
                            in1=h_hi[:, 2 * s:2 * s + 2, :].bitcast(F32), op0=ALU.mult,
                            op1=ALU.subtract).then_inc(turns.read["dve"], 1)
                for head in range(HEADS):
                    if j == SCORE[head] + 3:
                        keep_scores(head)
                for o in range(2):
                    for n in range(XC):
                        if j == U_OUT[o] - U_IN + OUT[o] * (n + 1) + 2:
                            out_to_x(o, n)
                if j == U_OUT[1] - U_IN + 6:
                    x_lo(2, 0)

            dve.memset(prm[:, 1, :], 0.0).then_inc(zeroed, 1)
            dve.memset(xbT[:, :, 0:3], 0.0)
            dve.memset(sc[:, :, :], 0.0)
            dve.wait_ge(mid_done, 1)
            dve.tensor_copy(pv[:, 0, 0:KT], mm[:, 0, 0:KT]).then_inc(mids.read["dve"], 1)
            dve.wait_ge(*mids.done(mids.at["gain",]))
            x_lo(0, 0)
            ffn(0)
            for j in range(MIX):
                split(U_IN + j, j % RING)
                mixer_side(j)
            ffn(1)

            def gate_pre(n):
                dve.wait_ge(unit_done, U_GATE + UD * (n + 1))
                pair = acc[accs.at["ple", n] % 2]
                for i in range(TILES):
                    ins = dve.scalar_tensor_tensor(out=zt[:, i, :], in0=pair[:, i, :], scalar=rs[:, 3, i:i + 1],
                                                   in1=ple_b[:, n * N:(n + 1) * N], op0=ALU.mult, op1=ALU.add)
                ins.then_inc(accs.read["dve"], 1)

            def gate_add(n):
                dve.wait_ge(sig_ready, n + 1)
                link(dve.tensor_tensor(zt[:, :, :], zt[:, :, :], proj[:, :, n * N:(n + 1) * N], ALU.mult))
                xn = x[:, :, n * N:(n + 1) * N]
                dve.tensor_tensor(xn, xn, zt[:, :, :], ALU.add).then_inc(x_final, 1)
                dve.wait_ge(x_final, n + 1)

            def final_gain(i, n):
                part_x = slice(n * N, (n + 1) * N)
                return dve.tensor_tensor(proj[:, i, part_x], x[:, i, part_x], fin_g[:, part_x], ALU.mult)

            for j in range(XC + UD * XC):
                split(U_PROJ + j, j % RING)
                if j == 2:
                    down_to_x(1, 1, XC - 1)
                if j == 4:
                    x_lo(3, XC - 1)
                if j == 5:
                    row_factors(3)
                if j == 8:
                    dve.wait_ge(rs_ready, 4)
                    dve.wait_ge(*accs.done(accs.at["proj", XC - 1]))
                for n in range(XC - 1):
                    if j == XC + UD * n + 10:
                        gate_pre(n)
                    if j == XC + UD * n + 12:
                        gate_add(n)
                    if j == XC + UD * n + 13:
                        for i in range(TILES):
                            final_gain(i, n)
            last = slice(D - N, D)
            for i in range(TILES):
                dve.wait_ge(last_done, i + 1)
                dve.scalar_tensor_tensor(out=zt[:, i, :], in0=acc[accs.at["ple", XC - 1] % 2][:, i, :],
                                         scalar=rs[:, 3, i:i + 1], in1=ple_b[:, last], op0=ALU.mult,
                                         op1=ALU.add).then_inc(last_pre, 1)
                dve.wait_ge(sig_ready, XC + i)
                link(dve.tensor_tensor(zt[:, i, :], zt[:, i, :], proj[:, i, last], ALU.mult))
                dve.tensor_tensor(x[:, i, last], x[:, i, last], zt[:, i, :], ALU.add).then_inc(x_final, 1)
                dve.wait_ge(x_final, XC + i)
                final_gain(i, XC - 1).then_inc(scaled, 1)
                dve.wait_ge(squared, squared_at["final", i])
                link(dve.tensor_reduce(ms[:, 4, i:i + 1], ssq[:, 4, i, :], AX.X, ALU.add))
                dve.tensor_scalar(ms[:, 4, i:i + 1], ms[:, 4, i:i + 1], 1.0 / D, EPS, ALU.mult,
                                  ALU.add).then_inc(ms_ready, 1)
                dve.wait_ge(rs_ready, 5 + i)
                dve.wait_ge(scaled, i + 1)
                dve.tensor_scalar(proj[:, i, 0:D // 2], proj[:, i, 0:D // 2], rs[:, 4, i:i + 1], None,
                                  ALU.mult).then_inc(final_dve, 1)

        @block.gpsimd
        def _(pool):
            pool.memset(mhalf[:, :], -0.5)
            pool.memset(masks[:, :, :], 1.0)
            pool.memset(ident[:, :], 0.0).then_inc(own_pool, 1)
            pool.wait_ge(own_pool, 1)
            pool.affine_select(out=ident[:, :], in_=ident[:, :], compare_op=ALU.not_equal, fill=1.0, base=0,
                               pattern=[[-1, P]], channel_multiplier=1).then_inc(consts, 1)
            for n, L in enumerate(LEVELS):
                view = masks[:, n, :].rearrange("p (n l) -> p n l", l=L)
                pool.affine_select(out=view, in_=view, compare_op=ALU.is_ge, fill=0.0, base=0,
                                   pattern=[[-2 * L, 64 // L], [0, L]], channel_multiplier=1)\
                    .then_inc(own_pool, 1)
                pool.wait_ge(own_pool, 2 + n)
                pool.affine_select(out=view, in_=view, compare_op=ALU.is_ge, fill=0.0, base=L - 1,
                                   pattern=[[2 * L, 64 // L], [0, L]], channel_multiplier=-1)\
                    .then_inc(consts, 1)
            for name, dst in (("lru_w_a", wa_sb), ("lru_w_x", wx_sb)):
                pool.dma_start(dst.rearrange("c (n d) -> c n d", n=NB), A[name].rearrange("l n c d -> c (l n) d"))\
                    .then_inc(lru_w_in, 16)

            def power(nu):
                pool.wait_ge(ms_ready, nu + 1)
                pool.tensor_tensor(rs[:, nu, :], ms[:, nu, :], mhalf[:, 0:TILES], ALU.pow).then_inc(rs_ready, 1)

            power(0)
            power(1)
            for s in range(HEADS // 2):
                pool.wait_ge(oms_ready, s + 1)
                pool.tensor_tensor(ors[:, 2 * s:2 * s + 2, :].rearrange("p a b -> p (a b)"),
                                   oms[:, 2 * s:2 * s + 2, :].rearrange("p a b -> p (a b)"), mhalf[:, :],
                                   ALU.pow).then_inc(ors_ready, 1)
            pool.wait_ge(turned, turns.at["diag", HEADS - 1] + 1)
            pool.dma_start(p_sb, p_dram).then_inc(late_in, 16)
            pool.dma_start(ple_b, A["ple_b_gate"].to_broadcast([P, D])).then_inc(late_in, 16)
            pool.dma_start(fin_g, A["final_norm"].rearrange("(a d) -> a d", a=1).to_broadcast([P, D]))\
                .then_inc(late_in, 16)
            power(2)
            power(3)
            for i in range(TILES):
                pool.wait_ge(ms_ready, 5 + i)
                pool.tensor_tensor(rs[:, 4, i:i + 1], ms[:, 4, i:i + 1], mhalf[:, 0:1], ALU.pow).then_inc(rs_ready, 1)


_INS = ["x", "p", "ffn1_norm", "ffn1_w_gate", "ffn1_w_up", "ffn1_w_down", "mix_norm", "w_in",
        "hgrn_lower_bounds", "hgrn_g_norm", "conv_w", "conv_b", "lru_w_a", "lru_b_a", "lru_w_x", "lru_b_x",
        "lru_lambda", "w_out", "ffn2_norm", "ffn2_w_gate", "ffn2_w_up", "ffn2_w_down", "ple_norm",
        "ple_w_gate", "ple_b_gate", "ple_w_proj", "final_norm"]


def kernel(**inputs):
    import numpy as _np
    import concourse.bacc as _bacc
    from concourse import mybir as _mybir
    from concourse.bass_utils import run_bass_kernel_spmd as _run

    nc = _bacc.Bacc("TRN2", target_bir_lowering=False, num_devices=1)
    arrays, args = {}, {}
    for name in _INS:
        a = _np.ascontiguousarray(inputs[name])
        arrays[f"in_{name}_dram"] = a
        args[name] = nc.dram_tensor(f"in_{name}_dram", a.shape, _mybir.dt.from_np(a.dtype), kind="ExternalInput").ap()
    shape = inputs["x"].shape
    out = nc.dram_tensor("out_dram", shape, _mybir.dt.float32, kind="ExternalOutput").ap()
    block_kernel(nc, args, out)
    r = _run(nc, [arrays], core_ids=[0])
    return r.results[0]["out_dram"]
```
